# Optimizing a Trainium2 kernel written in Bass

```python
import math
import jax, jax.numpy as jnp
from jax import lax
import numpy as np

D_MODEL = 2048
BATCH = 1
SEQ = 256
DEPTH = 2

N_MIXERS = 2
HEAD_DIM = 128
FOX_HEADS = D_MODEL // HEAD_DIM
DIFF_HEADS = D_MODEL // (2 * HEAD_DIM)
D_FF = 256 * ((8 * D_MODEL // 3 + 255) // 256)
CONV_WIDTH = 3
NUM_BUCKETS = 32
MAX_DISTANCE = 128
Q_BLOCK = 128
NORM_EPS = 1e-6
SUBLN_EPS = 1e-5
N_FOX = (DEPTH + 1) // 2
N_DIFF = DEPTH // 2

kernel_name = "hybrid_fox_diffattn_convffn"

def rms_norm(x, g, eps=NORM_EPS):
    xf = x.astype(jnp.float32)
    y = xf * lax.rsqrt(jnp.mean(xf * xf, axis=-1, keepdims=True) + eps)
    return (y * g.astype(jnp.float32)).astype(x.dtype)

def t5_bucket(dist):
    n = jnp.maximum(dist, 0)
    max_exact = NUM_BUCKETS // 2
    nf = jnp.maximum(n, 1).astype(jnp.float32)
    large = max_exact + (jnp.log(nf / max_exact) / math.log(MAX_DISTANCE / max_exact)
                         * (NUM_BUCKETS - max_exact)).astype(jnp.int32)
    large = jnp.minimum(large, NUM_BUCKETS - 1)
    return jnp.where(n < max_exact, n, large)

def fox_attention(h, w_in, b_f, qk_norm, w_out):
    B, S, _ = h.shape
    nb = S // Q_BLOCK
    proj = h @ w_in
    q, k, v, gate, f_logit = jnp.split(proj, [D_MODEL, 2 * D_MODEL, 3 * D_MODEL, 4 * D_MODEL], axis=-1)
    q = rms_norm(q.reshape(B, S, FOX_HEADS, HEAD_DIM), qk_norm[0])
    k = rms_norm(k.reshape(B, S, FOX_HEADS, HEAD_DIM), qk_norm[1])
    v = v.reshape(B, S, FOX_HEADS, HEAD_DIM)
    log_f = jax.nn.log_sigmoid((f_logit + b_f).astype(jnp.float32))
    c = jnp.cumsum(log_f, axis=1).transpose(0, 2, 1)
    q_blk = jnp.moveaxis(q.reshape(B, nb, Q_BLOCK, FOX_HEADS, HEAD_DIM), 1, 0)
    c_blk = jnp.moveaxis(c.reshape(B, FOX_HEADS, nb, Q_BLOCK), 2, 0)
    key_pos = jnp.arange(S)
    scale = HEAD_DIM ** -0.5

    def block(args):
        qb, cb, bi = args
        q_pos = bi * Q_BLOCK + jnp.arange(Q_BLOCK)
        logits = jnp.einsum('bqhd,bkhd->bhqk', qb, k).astype(jnp.float32) * scale
        decay = cb[..., :, None] - c[..., None, :]
        causal = key_pos[None, :] <= q_pos[:, None]
        logits = jnp.where(causal, logits + decay, -jnp.inf)
        p = jax.nn.softmax(logits, axis=-1).astype(v.dtype)
        return jnp.einsum('bhqk,bkhd->bqhd', p, v)

    o = lax.map(block, (q_blk, c_blk, jnp.arange(nb)))
    o = jnp.moveaxis(o, 0, 1).reshape(B, S, D_MODEL)
    o = o * jax.nn.sigmoid(gate)
    return o @ w_out

def diff_attention(h, w_in, lam, subln, w_out, rel_bias, lambda_init):
    B, S, _ = h.shape
    nb = S // Q_BLOCK
    q, k, v = jnp.split(h @ w_in, 3, axis=-1)
    q = q.reshape(B, S, DIFF_HEADS, 2, HEAD_DIM)
    k = k.reshape(B, S, DIFF_HEADS, 2, HEAD_DIM)
    v = v.reshape(B, S, DIFF_HEADS, 2 * HEAD_DIM)
    lamf = lam.astype(jnp.float32)
    lam_full = (jnp.exp(jnp.sum(lamf[0] * lamf[1])) - jnp.exp(jnp.sum(lamf[2] * lamf[3]))
                + lambda_init)
    q_blk = jnp.moveaxis(q.reshape(B, nb, Q_BLOCK, DIFF_HEADS, 2, HEAD_DIM), 1, 0)
    key_pos = jnp.arange(S)
    scale = HEAD_DIM ** -0.5

    def block(args):
        qb, bi = args
        q_pos = bi * Q_BLOCK + jnp.arange(Q_BLOCK)
        logits = jnp.einsum('bqhjd,bkhjd->bhjqk', qb, k).astype(jnp.float32) * scale
        bias = rel_bias[t5_bucket(q_pos[:, None] - key_pos[None, :])]
        bias = bias.transpose(2, 3, 0, 1).astype(jnp.float32)
        causal = key_pos[None, :] <= q_pos[:, None]
        logits = jnp.where(causal, logits + bias, -jnp.inf)
        p = jax.nn.softmax(logits, axis=-1)
        a = p[:, :, 0] - lam_full * p[:, :, 1]
        return jnp.einsum('bhqk,bkhd->bqhd', a.astype(v.dtype), v)

    o = lax.map(block, (q_blk, jnp.arange(nb)))
    o = jnp.moveaxis(o, 0, 1).reshape(B, S, DIFF_HEADS, 2 * HEAD_DIM)
    o = rms_norm(o, subln, SUBLN_EPS) * (1.0 - lambda_init)
    return o.reshape(B, S, D_MODEL) @ w_out

def conv_ffn(h, w_in, conv_w, conv_b, w_out):
    g, u = jnp.split(h @ w_in, 2, axis=-1)
    g = lax.conv_general_dilated(g, conv_w[:, None, :], window_strides=(1,),
                                 padding=[(CONV_WIDTH - 1, 0)],
                                 dimension_numbers=('NWC', 'WIO', 'NWC'),
                                 feature_group_count=D_FF) + conv_b
    return (jax.nn.gelu(g, approximate=False) * u) @ w_out

def setup_inputs(seed: int = 0) -> dict:
    key = jax.random.key(seed)
    ks = jax.random.split(key, 20)
    n = jax.random.normal
    D, F = D_MODEL, D_FF
    return {
        "x": n(ks[0], (BATCH, SEQ, D), jnp.float32),
        "attn_norm": 1.0 + 0.02 * n(ks[1], (DEPTH, D), jnp.float32),
        "ffn_norm": 1.0 + 0.02 * n(ks[2], (DEPTH, D), jnp.float32),
        "final_norm": 1.0 + 0.02 * n(ks[3], (D,), jnp.float32),
        "fox_w_in": n(ks[4], (N_FOX, D, 4 * D + FOX_HEADS), jnp.float32) * D ** -0.5,
        "fox_b_f": jax.random.uniform(ks[5], (N_FOX, FOX_HEADS), jnp.float32, 1.0, 4.0),
        "fox_qk_norm": 1.0 + 0.02 * n(ks[6], (N_FOX, 2, HEAD_DIM), jnp.float32),
        "fox_w_out": n(ks[7], (N_FOX, D, D), jnp.float32) * D ** -0.5,
        "diff_w_in": n(ks[8], (N_DIFF, D, 3 * D), jnp.float32) * D ** -0.5,
        "diff_lambda": 0.1 * n(ks[9], (N_DIFF, 4, HEAD_DIM), jnp.float32),
        "diff_subln": 1.0 + 0.02 * n(ks[10], (N_DIFF, 2 * HEAD_DIM), jnp.float32),
        "diff_w_out": n(ks[11], (N_DIFF, D, D), jnp.float32) * D ** -0.5,
        "rel_bias": 0.5 * n(ks[12], (NUM_BUCKETS, DIFF_HEADS, 2), jnp.float32),
        "ffn_w_in": n(ks[13], (DEPTH, D, 2 * F), jnp.float32) * D ** -0.5,
        "ffn_conv_w": n(ks[14], (DEPTH, CONV_WIDTH, F), jnp.float32) * CONV_WIDTH ** -0.5,
        "ffn_conv_b": 0.02 * n(ks[15], (DEPTH, F), jnp.float32),
        "ffn_w_out": n(ks[16], (DEPTH, F, D), jnp.float32) * F ** -0.5,
    }

def reference(x, attn_norm, ffn_norm, final_norm, fox_w_in, fox_b_f, fox_qk_norm, fox_w_out,
              diff_w_in, diff_lambda, diff_subln, diff_w_out, rel_bias,
              ffn_w_in, ffn_conv_w, ffn_conv_b, ffn_w_out):
    h = x
    for i in range(DEPTH):
        j = i // N_MIXERS
        a_in = rms_norm(h, attn_norm[i])
        if i % N_MIXERS == 0:
            h = h + fox_attention(a_in, fox_w_in[j], fox_b_f[j], fox_qk_norm[j], fox_w_out[j])
        else:
            lambda_init = 0.8 - 0.6 * math.exp(-0.3 * i)
            h = h + diff_attention(a_in, diff_w_in[j], diff_lambda[j], diff_subln[j],
                                   diff_w_out[j], rel_bias, lambda_init)
        h = h + conv_ffn(rms_norm(h, ffn_norm[i]), ffn_w_in[i], ffn_conv_w[i], ffn_conv_b[i], ffn_w_out[i])
    return rms_norm(h, final_norm)


_drawn_inputs = setup_inputs


def setup_inputs(seed=0):
    import zlib

    import numpy as np

    out = dict(_drawn_inputs(seed))
    spreads = {}
    factors = {'attn_norm': 2.865,
     'final_norm': 2.94,
     'fox_qk_norm': 8.0,
     'diff_subln': 5.34,
     'ffn_conv_b': 3.455}
    for name, (base, spread) in spreads.items():
        noise = np.random.default_rng([zlib.crc32(name.encode()), seed]).standard_normal(out[name].shape)
        drawn = base * np.exp(spread * noise) if base else spread * noise
        out[name] = __import__('jax').numpy.asarray(drawn.astype(out[name].dtype))
    for name, factor in factors.items():
        out[name] = (out[name] * factor).astype(out[name].dtype)
    return out
```

```python
import math
from contextlib import ExitStack

import numpy as np
import concourse.bass as bass
import concourse.mybir as mybir

F32 = mybir.dt.float32
F32R = mybir.dt.float32r
ALU = mybir.AluOpType
ACT = mybir.ActivationFunctionType
AX = mybir.AxisListType

P = 128
SEQ = 256
TT = SEQ // P
D = 2048
DC = D // P
HEADS = D // P
F = 256 * ((8 * D // 3 + 255) // 256)
FC = F // P
BUCKETS = 32
MAX_DISTANCE = 128
DEPTH = 2
BLOCK = 256
UK = 4
RING = 4
PAIRS = D // BLOCK
D_SIZES = [UK] * (DC // UK)
OUT_UNITS = 12
F_SIZES = [UK] * (FC - 3 * OUT_UNITS) + [UK - 1] * (UK * OUT_UNITS - FC)
UD = len(D_SIZES)
assert sum(F_SIZES) == FC and len(F_SIZES) == OUT_UNITS and UD == RING and OUT_UNITS % RING == 0
SCORES = SEQ + P
NORM_EPS = 1e-6
SUBLN_EPS = 1e-5
MASKED = -1e30
SCALE = P ** -0.5
LAMBDA_INIT = 0.8 - 0.6 * math.exp(-0.3 * 1)
LINE = SEQ + P
FFN_BLOCKS = F // BLOCK

FOX_UNITS, DIFF_UNITS, GU_UNITS = 4 * UD, 3 * UD, 2 * UD
U_FOX = 0
U_FOX_OUT = U_FOX + PAIRS * FOX_UNITS
U_GU = [U_FOX_OUT + PAIRS * UD]
U_DOWN = [U_GU[0] + FFN_BLOCKS * GU_UNITS]
U_DIFF = U_DOWN[0] + PAIRS * OUT_UNITS
U_DIFF_OUT = U_DIFF + PAIRS * DIFF_UNITS
U_GU.append(U_DIFF_OUT + PAIRS * UD)
U_DOWN.append(U_GU[1] + FFN_BLOCKS * GU_UNITS)
UNITS = U_DOWN[1] + PAIRS * OUT_UNITS

B_FOX = 0
B_DIFF = B_FOX + 4 * PAIRS
B_ALL = B_DIFF + 3 * PAIRS

V_ATTN, V_FFN, V_FINAL, V_QK, V_SUBLN, V_LAM = 0, 2 * DC, 4 * DC, 5 * DC, 5 * DC + 2, 5 * DC + 4
VROWS = V_LAM + 4
assert 2 * FC == VROWS
FIRST_SPLITS = [1, 3, 4, 5]
VTILES = 1 + 2 * DEPTH


def v_conv(layer, tap):
    return VROWS * (1 + 2 * layer) + FC * tap


def bucket_table():
    table = np.zeros((BUCKETS + 1, LINE), np.float32)
    exact = BUCKETS // 2
    for m in range(LINE):
        n = m - (P - 1)
        if n < 0:
            table[BUCKETS, m] = MASKED
        elif n < exact:
            table[n, m] = 1.0
        else:
            large = exact + int(math.log(n / exact) / math.log(MAX_DISTANCE / exact) * (BUCKETS - exact))
            table[min(large, BUCKETS - 1), m] = 1.0
    return table


def trunk(nc, x, attn_norm, ffn_norm, final_norm, fox_w_in, fox_b_f, fox_qk_norm, fox_w_out, diff_w_in, diff_lambda,
          diff_subln, diff_w_out, rel_bias, ffn_w_in, ffn_conv_w, ffn_conv_b, ffn_w_out, buckets, out):
    ctx = ExitStack()

    start = (nc.sbuf_base + 63) // 64 * 64
    top = [start]

    def sb(name, shape, dtype=F32, at=None):
        size = 4 * int(np.prod(shape[1:]))
        if at is None:
            at = top[0]
            top[0] += (size + 31) // 32 * 32
        return nc.alloc_sbuf_tensor_at(name, shape, dtype, offset=at)

    residual = sb("residual", [P, DC, SEQ])
    tokens_at = top[0]
    in_hi = sb("in_hi", [P, DC, SEQ], F32R)
    in_lo = sb("in_lo", [P, DC, SEQ], F32R)
    token_major = sb("token_major", [P, TT, D], at=tokens_at)
    raw = sb("raw", [P, RING, UK, BLOCK])
    w_hi = sb("w_hi", [P, RING, UK, BLOCK], F32R)
    w_lo = sb("w_lo", [P, RING, UK, BLOCK], F32R)
    vectors = sb("vectors", [P, VTILES * VROWS])
    identity = sb("identity", [P, P])
    ones = sb("ones", [P, P])
    rstd = sb("rstd", [P, SEQ])
    rstd_col = sb("rstd_col", [P, TT])
    square_sum = sb("square_sum", [P, 2, SEQ])
    squares = sb("squares", [P, 2, SEQ])
    logs = sb("logs", [P, 2, SEQ])
    guess = sb("guess", [P, 2, SEQ])
    mean_sq = sb("mean_sq", [P, 2, SEQ])
    small = sb("small", [P, 32])
    scaled = sb("scaled", [P, 4])
    bias_tile = sb("bias_tile", [P, 2, SEQ])
    region = top[0]
    heads_hi = sb("heads_hi", [P, DC, SEQ], F32R)
    heads_lo = sb("heads_lo", [P, DC, SEQ], F32R)
    rows16_at = top[0]
    x_rows = sb("x_rows", [P, TT, D])
    neg_c = sb("neg_c", [HEADS, HEADS, SEQ], at=rows16_at)
    q_raw = sb("q_raw", [P, 2, SEQ])
    k_raw = sb("k_raw", [P, 2, SEQ])
    q_norm = sb("q_norm", [P, 2, SEQ])
    k_norm = sb("k_norm", [P, 2, SEQ])
    head_rstd = sb("head_rstd", [P, 2, SEQ])
    gate = sb("gate", [P, 2, SEQ])
    gate_exp = sb("gate_exp", [P, 2, SEQ])
    gate_sig = sb("gate_sig", [P, 2, SEQ])
    logits_at = top[0]
    logits = sb("logits", [P, 2, SCORES])
    vector_rows = sb("vector_rows", [P, VTILES, P], at=logits_at)
    expd = sb("expd", [P, 2, SCORES])
    probs = sb("probs", [P, 2, SCORES])
    probs_t = sb("probs_t", [P, 2, SCORES])
    attended = sb("attended", [P, 2, SEQ])
    values = sb("values", [P, TT, BLOCK])
    mask = sb("mask", [P, SCORES])
    c_col = sb("c_col", [P, TT, HEADS])
    neg_max = sb("neg_max", [P, 4])
    exp_sum = sb("exp_sum", [P, 4])
    inv_sum = sb("inv_sum", [P, 4])
    inv_lam = sb("inv_lam", [P, 4])
    f_raw = sb("f_raw", [P, DC, HEADS])
    f_work = sb("f_work", [HEADS, 4, SEQ])
    table = sb("table", [BUCKETS + 1, LINE])
    rel = sb("rel", [BUCKETS + 1, HEADS])
    lines = sb("lines", [HEADS, LINE])
    attention_top = top[0]
    top[0] = region
    hidden_hi = sb("hidden_hi", [P, FC, SEQ], F32R)
    hidden_lo = sb("hidden_lo", [P, FC, SEQ], F32R)
    g_pad = sb("g_pad", [P, 2, SEQ + 2])
    conv = sb("conv", [P, 2, SEQ])
    up = sb("up", [P, 2, SEQ])
    region_top = max(attention_top, top[0])
    assert region_top <= nc.sbuf_usable_end, (region_top, nc.sbuf_usable_end)
    final_g = sb("final_g", [P, 2, SEQ], at=tokens_at + 4 * DC * SEQ)

    def pb(name, shape):
        return ctx.enter_context(nc.psum_tensor(name, shape, F32))

    acc = [pb("acc_even", [P, 2, 512]), pb("acc_odd", [P, 2, 512])]
    score_ps = pb("score_ps", [P, 2, 512])
    sum_ps = pb("sum_ps", [P, 512])
    out_ps = pb("out_ps", [P, 512])

    line_dram = nc.dram_tensor("line_dram", [HEADS, LINE], F32, kind="Internal")

    def sem(name):
        return ctx.enter_context(nc.semaphore(name))

    landed = [sem(f"landed{s}") for s in range(RING)]
    hi_ready = sem("hi_ready")
    lo_ready = sem("lo_ready")
    multiplied = sem("multiplied")
    drained = sem("drained")
    rows_landed = sem("rows_landed")
    x_landed = sem("x_landed")
    misc_landed = sem("misc_landed")
    const_ready = sem("const_ready")
    const_base = sem("const_base")
    vectors_t = sem("vectors_t")
    vectors_ready = sem("vectors_ready")
    x_t = sem("x_t")
    x_updated = sem("x_updated")
    squared = sem("squared")
    sum_updated = sem("sum_updated")
    in_hi_ready = sem("in_hi_ready")
    in_ready = sem("in_ready")
    sums_ready = sem("sums_ready")

    def norm_sems(kind):
        return {step: sem(f"{kind}_{step}") for step in ("log", "guess", "guess_sq", "mean", "half")}

    token_norm, q_norm_sems, k_norm_sems, sub_norm_sems = (norm_sems(x) for x in ("token", "q", "k", "sub"))
    rstd_ready = sem("rstd_ready")
    q_rstd = sem("q_rstd")
    k_rstd = sem("k_rstd")
    col_ready = sem("col_ready")
    rstd_col_ready = sem("rstd_col_ready")
    scaled_ready = sem("scaled_ready")
    lam_prod = sem("lam_prod")
    lam_sum = sem("lam_sum")
    lam_exp = sem("lam_exp")
    lam_step = sem("lam_step")
    f_zero = sem("f_zero")
    f_hi = sem("f_hi")
    f_lo = sem("f_lo")
    f_mult = sem("f_mult")
    f_abs = sem("f_abs")
    f_step = sem("f_step")
    f_act = sem("f_act")
    f_t = sem("f_t")
    c_ready = sem("c_ready")
    rel_one = sem("rel_one")
    line_mult = sem("line_mult")
    line_ready = sem("line_ready")
    line_stored = sem("line_stored")
    bias_landed = sem("bias_landed")
    q_squared = sem("q_squared")
    k_squared = sem("k_squared")
    q_sums = sem("q_sums")
    k_sums = sem("k_sums")
    q_ready = sem("q_ready")
    k_ready = sem("k_ready")
    gate_exped = sem("gate_exped")
    gate_step = sem("gate_step")
    gate_ready = sem("gate_ready")
    scores_done = sem("scores_done")
    logits_done = sem("logits_done")
    max_done = sem("max_done")
    exp_done = sem("exp_done")
    inv_done = sem("inv_done")
    lam_scaled = sem("lam_scaled")
    probs_part = sem("probs_part")
    probs_done = sem("probs_done")
    probs_turned = sem("probs_turned")
    probs_t_ready = sem("probs_t_ready")
    attended_ps = sem("attended_ps")
    attended_done = sem("attended_done")
    sub_copied = sem("sub_copied")
    sub_squared = sem("sub_squared")
    sub_sums = sem("sub_sums")
    sub_rstd = sem("sub_rstd")
    heads_hi_ready = sem("heads_hi_ready")
    heads_ready = sem("heads_ready")
    pad_zero = sem("pad_zero")
    g_ready = sem("g_ready")
    tap0 = sem("tap0")
    tap1 = sem("tap1")
    tap2 = sem("tap2")
    gelu_done = sem("gelu_done")
    up_ready = sem("up_ready")
    product = sem("product")
    hidden_hi_ready = sem("hidden_hi_ready")
    hidden_ready = sem("hidden_ready")
    final_scaled = sem("final_scaled")
    final_t = sem("final_t")
    final_copied = sem("final_copied")
    final_done = sem("final_done")
    final_done_act = sem("final_done_act")
    stored = sem("stored")

    block = ctx.enter_context(nc.Block())

    @block.sync
    def _(sp):
        sp.dma_start(x_rows[:, :, :], x[0].rearrange("(t p) d -> p t d", p=P)).then_inc(x_landed, 16)
        sp.wait_ge(rows_landed, 16 * 13)

        def load(const, i, stride, weights, k0, nk, column):
            s = const % RING
            sp.wait_ge(lo_ready, const + i * stride + 1)
            src = weights.rearrange("(k p) n -> p k n", p=P)
            sp.dma_start(raw[:, s, 0:nk, :], src[:, k0:k0 + nk, bass.ds(column, BLOCK)]).then_inc(landed[s], 16)

        def load_block(const, i, stride, weights, sizes, column):
            k = 0
            for j, nk in enumerate(sizes):
                load(const + j, i, stride, weights, k, nk, column)
                k += nk

        def load_pairs(unit0, per, weights, first_columns, peeled):
            def body(i):
                for b, column in enumerate(first_columns):
                    load_block(unit0 + b * UD, i, per, weights, D_SIZES, i * BLOCK + column)
            if peeled:
                body(0)
            with sp.Fori(1 if peeled else 0, D // BLOCK) as i:
                body(i)

        load_pairs(U_FOX, FOX_UNITS, fox_w_in[0], [0, D, 3 * D, 2 * D], True)
        load_pairs(U_FOX_OUT, UD, fox_w_out[0], [0], False)
        for layer in range(DEPTH):
            if layer == 1:
                load_pairs(U_DIFF, DIFF_UNITS, diff_w_in[0], [0, D, 2 * D], False)
                load_pairs(U_DIFF_OUT, UD, diff_w_out[0], [0], False)
            with sp.Fori(0, FFN_BLOCKS) as i:
                load_block(U_GU[layer], i, GU_UNITS, ffn_w_in[layer], D_SIZES, i * BLOCK)
                load_block(U_GU[layer] + UD, i, GU_UNITS, ffn_w_in[layer], D_SIZES, i * BLOCK + F)
            with sp.Fori(0, PAIRS) as i:
                load_block(U_DOWN[layer], i, OUT_UNITS, ffn_w_out[layer], F_SIZES, i * BLOCK)
        sp.wait_ge(final_done, 1)
        sp.dma_start(out[0, P:SEQ, :], token_major[:, 1, :]).then_inc(stored, 16)
        sp.wait_ge(stored, 32)

    @block.gpsimd
    def _(pool):
        pool.memset(identity[:, :], 0.0).then_inc(const_base, 1)
        pool.memset(mask[:, :], 0.0).then_inc(const_base, 1)
        pool.memset(ones[:, :], 1.0).then_inc(const_ready, 1)
        pool.wait_ge(const_ready, 1)
        pool.memset(rel[BUCKETS:BUCKETS + 1, :], 1.0).then_inc(rel_one, 1)
        pool.wait_ge(rel_one, 1)
        pool.memset(heads_hi[:, :, 0:P].bitcast(F32), 0.0).then_inc(f_zero, 1)
        pool.memset(heads_lo[:, :, 0:P].bitcast(F32), 0.0).then_inc(f_zero, 1)
        pool.wait_ge(const_base, 2)
        pool.affine_select(out=identity[:, :], in_=identity[:, :], compare_op=ALU.not_equal, fill=1.0, base=0,
                           pattern=[[-1, P]], channel_multiplier=1).then_inc(const_ready, 1)
        diagonals = mask[:, P:3 * P].rearrange("p (t k) -> p t k", t=2)
        pool.affine_select(out=diagonals, in_=diagonals, compare_op=ALU.is_ge, fill=MASKED, base=0,
                           pattern=[[0, 2], [-1, P]], channel_multiplier=1).then_inc(const_ready, 1)

        def load_bias(h):
            rows = line_dram.ap()[bass.ds(2 * h, 2), :]
            pool.dma_start(bias_tile[:, :, :], bass.AP(rows.tensor, rows.offset, [[1, P], [LINE, 2], [1, SEQ]]))\
                .then_inc(bias_landed, 16)

        pool.wait_ge(line_ready, 1)
        pool.dma_start(line_dram.ap(), lines[:, :]).then_inc(line_stored, 16)
        pool.wait_ge(line_stored, 16)
        load_bias(0)
        with pool.Fori(1, PAIRS) as h:
            pool.wait_ge(logits_done, PAIRS + h)
            load_bias(h)

    @block.tensor
    def _(pe):
        pe.sem_inc(multiplied, RING)
        pe.wait_ge(const_ready, 3)

        def unit_features(const, i, stride, k0, nk, last_k, x_hi, x_lo, bank):
            s = const % RING
            pe.wait_ge(lo_ready, RING + const + 1 + i * stride)
            for m in range(2):
                for kk in range(nk):
                    k, c = k0 + kk, slice(m * P, (m + 1) * P)
                    o = acc[bank][:, m, 0:SEQ]
                    pe.matmul(o, w_hi[:, s, kk, c], x_hi[:, k, :], start=(k == 0), stop=False)
                    pe.matmul(o, w_hi[:, s, kk, c], x_lo[:, k, :], start=False, stop=False)
                    mm = pe.matmul(o, w_lo[:, s, kk, c], x_hi[:, k, :], start=False, stop=(k == last_k))
            mm.then_inc(multiplied, 1)

        def unit_tokens(const, i, stride, k0, nk, last_k, bank):
            s = const % RING
            pe.wait_ge(lo_ready, RING + const + 1 + i * stride)
            for t in range(TT):
                for kk in range(nk):
                    k, c = k0 + kk, slice(t * P, (t + 1) * P)
                    o = acc[bank][:, t, 0:BLOCK]
                    pe.matmul(o, in_hi[:, k, c], w_hi[:, s, kk, :], start=(k == 0), stop=False)
                    pe.matmul(o, in_hi[:, k, c], w_lo[:, s, kk, :], start=False, stop=False)
                    mm = pe.matmul(o, in_lo[:, k, c], w_hi[:, s, kk, :], start=False, stop=(k == last_k))
            mm.then_inc(multiplied, 1)

        def norm_sums(stage):
            pe.wait_ge(sum_updated, (PAIRS + 1) * (stage + 1))
            for m in range(2):
                mm = pe.matmul(sum_ps[:, 0:SEQ], ones[:, :], square_sum[:, m, :], start=(m == 0), stop=(m == 1))
            mm.then_inc(sums_ready, 1)

        def norm_column(stage):
            pe.wait_ge(rstd_ready, stage + 1)
            for t in range(TT):
                mm = pe.matmul(out_ps[:, t:t + 1], rstd[0:1, t * P:(t + 1) * P], ones[0:1, 0:1], start=True, stop=True)
            mm.then_inc(col_ready, 1)

        pe.wait_ge(x_landed, 16)

        def turn_x(b):
            if b >= 2:
                pe.wait_ge(x_updated, b - 1)
            for m in range(2):
                for t in range(TT):
                    mm = pe.transpose(score_ps[:, b % 2, m * SEQ + t * P:m * SEQ + (t + 1) * P],
                                      x_rows[:, t, (2 * b + m) * P:(2 * b + m + 1) * P], identity[:, :])
            mm.then_inc(x_t, 1)

        turn_x(0)
        turn_x(1)
        pe.wait_ge(rows_landed, 16 * 13)
        for v in range(VTILES):
            mm = pe.transpose(acc[1][:, 0, v * VROWS:(v + 1) * VROWS], vector_rows[0:VROWS, v, :],
                              identity[0:VROWS, 0:VROWS])
        mm.then_inc(vectors_t, 1)

        def fox_scores(p):
            pe.wait_ge(q_ready, p + 1)
            pe.wait_ge(k_ready, p + 1)
            pe.wait_ge(c_ready, 2)
            for j in range(2):
                for q, keys, o in ((1, SEQ, 0), (0, P, SEQ)):
                    o = score_ps[:, j, o:o + keys]
                    pe.matmul(o, q_norm[:, j, q * P:(q + 1) * P], k_norm[:, j, 0:keys], start=True, stop=False)
                    head = neg_c[:, bass.ds(2 * p + j, 1), 0:keys].rearrange("r a k -> r (a k)")
                    mm = pe.matmul(o, ones[0:HEADS, :], head, start=False, stop=True)
            mm.then_inc(scores_done, 1)

        def turn_probs(p, n, heads):
            pe.wait_ge(probs_done, p + 1 + n)
            for j in range(heads):
                for o, c in ((0, SEQ), (P, 0), (2 * P, P)):
                    mm = pe.transpose(score_ps[:, j, o:o + P], probs[:, j, c:c + P], identity[:, :])
            mm.then_inc(probs_turned, 1)

        def attend(p, n, heads):
            pe.wait_ge(probs_t_ready, p + 1 + n)
            for j in range(2):
                src = j if heads == 2 else 0
                pe.matmul(out_ps[:, j * SEQ:(j + 1) * SEQ], values[:, 0, j * P:(j + 1) * P],
                          probs_t[:, src, 0:SEQ], start=True, stop=False)
                mm = pe.matmul(out_ps[:, j * SEQ + P:(j + 1) * SEQ], values[:, 1, j * P:(j + 1) * P],
                               probs_t[:, src, SEQ:SCORES], start=False, stop=True)
            mm.then_inc(attended_ps, 1)

        def fox_pair(i, first):
            u = U_FOX
            if not first:
                fox_scores(i - 1)
            for j in range(UD):
                if first:
                    if j < UD - 1:
                        turn_x(2 * j + 2)
                        turn_x(2 * j + 3)
                    pe.wait_ge(in_ready, 2 * j + 2)
                elif j == 0:
                    pe.wait_ge(drained, B_FOX + 4 * i - 1)
                unit_features(u + j, i, FOX_UNITS, UK * j, UK, DC - 1, in_hi, in_lo, 0)
                if first and j == 1:
                    pe.wait_ge(lam_prod, 1)
                    pe.matmul(acc[1][:, 1, 0:2], ones[:, :], small[:, 0:2], start=True, stop=True).then_inc(lam_sum, 1)
                    pe.wait_ge(misc_landed, 48)
                    pe.wait_ge(rel_one, 1)
                    pe.matmul(out_ps[0:HEADS, 0:LINE], rel[:, :], table[:, :], start=True, stop=True).then_inc(line_mult, 1)
            if first:
                norm_sums(0)
                pe.wait_ge(vectors_ready, 1)
                pe.wait_ge(lam_exp, 1)
                pe.wait_ge(line_ready, 1)
            for j in range(UD):
                if j == 0 and not first:
                    pe.wait_ge(drained, B_FOX + 4 * i)
                unit_features(u + 4 + j, i, FOX_UNITS, UK * j, UK, DC - 1, in_hi, in_lo, 1)
                if j == 0 and first:
                    norm_column(0)
                if j == (1 if first else 0):
                    if first:
                        pe.wait_ge(f_lo, 1)
                        pe.wait_ge(rstd_col_ready, 1)
                        for k in range(DC):
                            o = out_ps[:, 0:SEQ]
                            pe.matmul(o, heads_hi[:, k, 0:P], in_hi[:, k, :], start=(k == 0), stop=False)
                            pe.matmul(o, heads_hi[:, k, 0:P], in_lo[:, k, :], start=False, stop=False)
                            mm = pe.matmul(o, heads_lo[:, k, 0:P], in_hi[:, k, :], start=False, stop=(k == DC - 1))
                        mm.then_inc(f_mult, 1)
                    else:
                        turn_probs(i - 1, 0, 2)
                if j == 1:
                    pe.wait_ge(q_squared, i + 1)
                    if not first:
                        pe.wait_ge(k_norm_sems["mean"], i)
                    pe.matmul(sum_ps[:, :], ones[:, :], squares[:, :, :].rearrange("p m t -> p (m t)"),
                              start=True, stop=True).then_inc(q_sums, 1)
                if j == 2 and not first:
                    attend(i - 1, 0, 2)
            for j in range(UD):
                if j == 0:
                    pe.wait_ge(drained, B_FOX + 4 * i + 1)
                unit_features(u + 8 + j, i, FOX_UNITS, UK * j, UK, DC - 1, in_hi, in_lo, 0)
                if j == 1:
                    pe.wait_ge(k_squared, i + 1)
                    pe.wait_ge(q_norm_sems["mean"], i + 1)
                    pe.matmul(sum_ps[:, :], ones[:, :], squares[:, :, :].rearrange("p m t -> p (m t)"),
                              start=True, stop=True).then_inc(k_sums, 1)
            for j in range(UD):
                if j == 0:
                    pe.wait_ge(drained, B_FOX + 4 * i + 2)
                unit_tokens(u + 12 + j, i, FOX_UNITS, UK * j, UK, DC - 1, 1)
                if j == 0 and first:
                    pe.wait_ge(f_step, 5)
                    for t in range(TT):
                        mm = pe.transpose(out_ps[:, t * HEADS:(t + 1) * HEADS], f_work[:, 3, t * P:(t + 1) * P],
                                          identity[0:HEADS, 0:HEADS])
                    mm.then_inc(f_t, 1)

        fox_pair(0, True)
        with pe.Fori(1, PAIRS) as i:
            fox_pair(i, False)

        def attention_out(u, blocks_drained, in0, stage, turned, last_pair):
            def two_blocks(i, first):
                for b in range(2):
                    for j in range(UD):
                        if j == 0 and first:
                            pe.wait_ge(drained, blocks_drained)
                        elif j == 0:
                            pe.wait_ge(x_updated, PAIRS * stage + 2 * i + b - 1)
                        if first and b == 0:
                            if j == 0:
                                pe.wait_ge(heads_ready, in0 + PAIRS - 1)
                            if j == 2:
                                turn_probs(PAIRS - 1, in0, turned)
                            if j == UD - 1:
                                last_pair()
                                pe.wait_ge(heads_ready, in0 + PAIRS)
                        unit_features(u + b * UD + j, i, 2 * UD, UK * j, UK, DC - 1, heads_hi, heads_lo, b)
            two_blocks(0, True)
            with pe.Fori(1, PAIRS // 2) as i:
                two_blocks(i, False)

        def fox_last():
            attend(PAIRS - 1, 0, 2)

        fox_scores(PAIRS - 1)
        attention_out(U_FOX_OUT, B_DIFF, 0, 1, 2, fox_last)

        def feed_forward(layer):
            stage = 1 + 2 * layer

            def hidden_block(i, first):
                for g in range(2):
                    for j in range(UD):
                        if j == 0 and first:
                            pe.wait_ge(x_updated, PAIRS * stage + PAIRS - 1 + g)
                        elif j == 0:
                            pe.wait_ge((g_ready, up_ready)[g], FFN_BLOCKS * layer + i)
                        if first and g == 0:
                            pe.wait_ge(in_ready, PAIRS * stage + 2 * j + 2)
                        unit_features(U_GU[layer] + g * UD + j, i, GU_UNITS, UK * j, UK, DC - 1, in_hi, in_lo, g)
                    if first and g == 0:
                        norm_sums(stage)

            hidden_block(0, True)
            with pe.Fori(1, FFN_BLOCKS) as i:
                hidden_block(i, False)

            def two_blocks(i, last):
                for b in range(2):
                    k = 0
                    for j, nk in enumerate(F_SIZES):
                        if j == 0 and isinstance(i, int):
                            pe.wait_ge((g_ready, up_ready)[b], FFN_BLOCKS * (layer + 1))
                        elif j == 0:
                            pe.wait_ge(x_updated, PAIRS * (stage + 1) + 2 * i + b - 1)
                        if b == 0 and isinstance(i, int):
                            pe.wait_ge(hidden_ready, FFN_BLOCKS * layer + (k + nk + 1) // 2)
                        unit_features(U_DOWN[layer] + b * OUT_UNITS + j, i, 2 * OUT_UNITS, k, nk, FC - 1, hidden_hi,
                                      hidden_lo, b)
                        k += nk
                        if layer == DEPTH - 1 and j == 3:
                            if b == 1:
                                final_turn(2 * i)
                            elif not isinstance(i, int):
                                final_turn(2 * i - 1)

            two_blocks(0, False)
            with pe.Fori(1, PAIRS // 2) as i:
                two_blocks(i, False)

        def final_turn(n):
            pe.wait_ge(final_scaled, n + 1)
            for t in range(TT):
                for m in range(2):
                    mm = pe.transpose(out_ps[:, t * BLOCK + m * P:t * BLOCK + (m + 1) * P],
                                      final_g[:, m, t * P:(t + 1) * P], identity[:, :])
            mm.then_inc(final_t, 1)

        feed_forward(0)

        def diff_scores(p):
            pe.wait_ge(drained, B_DIFF + 3 * p + 2)
            for j in range(2):
                for q, keys, o in ((1, SEQ, 0), (0, P, SEQ)):
                    mm = pe.matmul(score_ps[:, j, o:o + keys], q_raw[:, j, q * P:(q + 1) * P], k_raw[:, j, 0:keys],
                                   start=True, stop=True)
            mm.then_inc(scores_done, 1)

        def subln_sums(p):
            pe.wait_ge(sub_squared, p + 1)
            for m in range(2):
                mm = pe.matmul(sum_ps[:, 0:SEQ], ones[:, :], squares[:, m, :], start=(m == 0), stop=(m == 1))
            mm.then_inc(sub_sums, 1)

        def diff_head(i, first):
            u = U_DIFF
            if not first:
                diff_scores(i - 1)
            for j in range(UD):
                if j == 0 and first:
                    pe.wait_ge(x_updated, PAIRS * 2 + PAIRS - 1)
                elif j == 0:
                    pe.wait_ge(drained, B_DIFF + 3 * i)
                if first:
                    pe.wait_ge(in_ready, PAIRS * 2 + 2 * j + 2)
                unit_features(u + j, i, DIFF_UNITS, UK * j, UK, DC - 1, in_hi, in_lo, 0)
            if first:
                norm_sums(2)
            for j in range(UD):
                if j == 0 and first:
                    pe.wait_ge(x_updated, PAIRS * 2 + PAIRS)
                elif j == 0:
                    pe.wait_ge(drained, B_DIFF + 3 * i - 1)
                unit_features(u + 4 + j, i, DIFF_UNITS, UK * j, UK, DC - 1, in_hi, in_lo, 1)
                if j == 0 and first:
                    norm_column(2)
                if j == 0 and not first:
                    turn_probs(i - 1, PAIRS, 1)
                if j == 2 and not first:
                    attend(i - 1, PAIRS, 1)
            for j in range(UD):
                if j == 0:
                    pe.wait_ge(drained, B_DIFF + 3 * i + 1)
                unit_tokens(u + 8 + j, i, DIFF_UNITS, UK * j, UK, DC - 1, 0)
                if j == 1 and not first:
                    subln_sums(i - 1)

        diff_head(0, True)
        with pe.Fori(1, PAIRS) as i:
            diff_head(i, False)

        def diff_last():
            attend(PAIRS - 1, PAIRS, 1)
            subln_sums(PAIRS - 1)

        diff_scores(PAIRS - 1)
        attention_out(U_DIFF_OUT, B_ALL, PAIRS, 3, 1, diff_last)
        feed_forward(1)
        final_turn(PAIRS - 1)
        norm_sums(4)
        pe.wait_ge(final_copied, PAIRS + 1)
        norm_column(4)

    @block.scalar
    def _(act):
        act.dma_start(vector_rows[V_ATTN:V_ATTN + 2 * DC, 0, :],
                      attn_norm.rearrange("l (c p) -> (l c) p", p=P)).then_inc(rows_landed, 16)
        act.dma_start(vector_rows[V_FFN:V_FFN + 2 * DC, 0, :],
                      ffn_norm.rearrange("l (c p) -> (l c) p", p=P)).then_inc(rows_landed, 16)
        act.dma_start(vector_rows[V_FINAL:V_FINAL + DC, 0, :],
                      final_norm.rearrange("(c p) -> c p", p=P)).then_inc(rows_landed, 16)
        act.dma_start(vector_rows[V_QK:V_QK + 2, 0, :], fox_qk_norm[0]).then_inc(rows_landed, 16)
        act.dma_start(vector_rows[V_SUBLN:V_SUBLN + 2, 0, :],
                      diff_subln.rearrange("l (c p) -> (l c) p", p=P)).then_inc(rows_landed, 16)
        act.dma_start(vector_rows[V_LAM:V_LAM + 4, 0, :], diff_lambda[0]).then_inc(rows_landed, 16)
        for layer in range(DEPTH):
            taps = ffn_conv_w[layer].rearrange("w (c p) -> (w c) p", p=P)
            act.dma_start(vector_rows[0:2 * FC, 1 + 2 * layer, :], taps[0:2 * FC, :]).then_inc(rows_landed, 16)
            act.dma_start(vector_rows[0:FC, 2 + 2 * layer, :], taps[2 * FC:3 * FC, :]).then_inc(rows_landed, 16)
            act.dma_start(vector_rows[FC:2 * FC, 2 + 2 * layer, :],
                          ffn_conv_b[layer].rearrange("(c p) -> c p", p=P)).then_inc(rows_landed, 16)
        act.dma_start(small[0:HEADS, 8:9], fox_b_f.rearrange("a h -> h a")).then_inc(rows_landed, 16)
        act.dma_start(f_raw[:, :, :],
                      fox_w_in[0].rearrange("(k p) n -> p k n", p=P)[:, :, 4 * D:4 * D + HEADS]).then_inc(misc_landed, 16)
        act.dma_start(table[:, :], buckets).then_inc(misc_landed, 16)
        act.dma_start(rel[0:BUCKETS, :], rel_bias.rearrange("b h j -> b (h j)")).then_inc(misc_landed, 16)
        act.preload_act_table_set("natural_log_exp_and_others")

        def split(const, i, stride, nk):
            s = const % RING
            act.wait_ge(landed[s], 16 * (const // RING + 1) + i * (16 * stride // RING))
            act.wait_ge(multiplied, const + 1 + i * stride)
            act.activation(w_hi[:, s, 0:nk, :], raw[:, s, 0:nk, :], ACT.Copy).then_inc(hi_ready, 1)

        def guess_rstd(sems, count, wide):
            log, first, mean = (t[:, 0:wide, :] for t in (logs, guess, mean_sq))
            act.wait_ge(sems["mean"], count)
            act.activation(log, mean, ACT.Ln).then_inc(sems["log"], 1)
            act.wait_ge(sems["log"], count)
            act.activation(first, log, ACT.Exp, scale=-0.5).then_inc(sems["guess"], 1)
            act.wait_ge(sems["guess"], count)
            act.activation(log, first, ACT.Square).then_inc(sems["guess_sq"], 1)

        def norm(stage):
            guess_rstd(token_norm, stage + 1, 1)

        def residual_pair(stage, b, g_column):
            act.wait_ge(x_updated, PAIRS * stage + 1 + b)
            act.wait_ge(sum_updated, (PAIRS + 1) * stage + 1 + b)
            act.activation(squares[:, :, :], residual[:, bass.ds(2 * b, 2), :], ACT.Square).then_inc(squared, 1)
            for m in range(2):
                ins = act.activation(in_hi[:, bass.ds(2 * b + m, 1), :], residual[:, bass.ds(2 * b + m, 1), :],
                                     ACT.Copy, scale=vectors[:, bass.ds(2 * b + (g_column + m), 1)])
            ins.then_inc(in_hi_ready, 1)

        act.wait_ge(const_ready, 3)
        act.wait_ge(vectors_ready, 1)
        for b in range(PAIRS):
            residual_pair(0, b, V_ATTN)
            if b in FIRST_SPLITS:
                split(FIRST_SPLITS.index(b), 0, 0, UK)
        act.wait_ge(lam_sum, 1)
        act.activation(small[:, 2:4], acc[1][:, 1, 0:2], ACT.Exp).then_inc(lam_exp, 1)
        act.wait_ge(misc_landed, 48)
        act.wait_ge(f_zero, 2)
        act.activation(heads_hi[:, :, 0:HEADS], f_raw[:, :, :], ACT.Copy).then_inc(f_hi, 1)

        def exponents(p, n):
            act.wait_ge(max_done, p + 1 + n)
            for j in range(2):
                act.activation(expd[:, j, 0:SEQ], logits[:, j, 0:SEQ], ACT.Exp, bias=neg_max[:, j:j + 1],
                               accum_out=exp_sum[:, j:j + 1])
                ins = act.activation(expd[:, j, SEQ:SCORES], logits[:, j, SEQ:SCORES], ACT.Exp,
                                     bias=neg_max[:, 2 + j:3 + j], accum_out=exp_sum[:, 2 + j:3 + j])
            ins.then_inc(exp_done, 1)

        def copy_probs(p, n, heads):
            act.wait_ge(probs_turned, p + 1 + n)
            act.activation(probs_t[:, 0:heads, :], score_ps[:, 0:heads, 0:SCORES], ACT.Copy).then_inc(probs_t_ready, 1)

        def heads_part(p, n):
            act.wait_ge(attended_done, p + 1 + n)
            act.activation(heads_hi[:, bass.ds(2 * p, 2), :], attended[:, :, :], ACT.Copy).then_inc(heads_hi_ready, 1)

        def fox_pair(i, first):
            for j in range(FOX_UNITS):
                split(U_FOX + RING + j, i, FOX_UNITS, UK)
                if first and j == 3:
                    norm(0)
                if j == 0 and not first:
                    exponents(i - 1, 0)
                if j == 4:
                    act.wait_ge(drained, B_FOX + 1 + 4 * i)
                    act.activation(squares[:, :, :], q_raw[:, :, :], ACT.Square).then_inc(q_squared, 1)
                if j == 5 and not first:
                    copy_probs(i - 1, 0, 2)
                if j == 6:
                    if not first:
                        act.wait_ge(k_ready, i)
                    guess_rstd(q_norm_sems, i + 1, 2)
                if j == 8:
                    act.wait_ge(drained, B_FOX + 2 + 4 * i)
                    act.activation(squares[:, :, :], k_raw[:, :, :], ACT.Square).then_inc(k_squared, 1)
                if j == 9:
                    if first:
                        act.wait_ge(f_abs, 1)
                        act.activation(f_work[:, 1, :], f_work[:, 0, :], ACT.Abs).then_inc(f_act, 1)
                        act.wait_ge(f_act, 1)
                        act.activation(f_work[:, 2, :], f_work[:, 1, :], ACT.Exp, scale=-1.0).then_inc(f_act, 1)
                        act.wait_ge(f_act, 2)
                        act.activation(f_work[:, 1, :], f_work[:, 2, :], ACT.Ln, bias=1.0).then_inc(f_act, 1)
                    else:
                        heads_part(i - 1, 0)
                if j == 10:
                    act.wait_ge(q_ready, i + 1)
                    guess_rstd(k_norm_sems, i + 1, 2)
                if j == 12:
                    act.wait_ge(drained, B_FOX + 3 + 4 * i)
                    act.activation(gate_exp[:, :, :], gate[:, :, :], ACT.Exp, scale=-1.0).then_inc(gate_exped, 1)

        fox_pair(0, True)
        with act.Fori(1, PAIRS) as i:
            fox_pair(i, False)

        def attention_out(u, stage, g_column, first_extra):
            def two_blocks(i, first):
                for b in range(2):
                    for j in range(UD):
                        split(u + RING + b * UD + j, i, 2 * UD, UK)
                        if first and b == 0:
                            first_extra(j)
                    residual_pair(stage, 2 * i + b, g_column)
            two_blocks(0, True)
            with act.Fori(1, PAIRS // 2) as i:
                two_blocks(i, False)

        def fox_last(j):
            if j == 0:
                exponents(PAIRS - 1, 0)
            if j == 1:
                copy_probs(PAIRS - 1, 0, 2)
            if j == 2:
                heads_part(PAIRS - 1, 0)

        attention_out(U_FOX_OUT, 1, V_FFN, fox_last)

        def feed_forward(layer):
            stage = 1 + 2 * layer
            n0 = FFN_BLOCKS * layer

            def hidden_block(i, first):
                for j in range(GU_UNITS):
                    split(U_GU[layer] + RING + j, i, GU_UNITS, UK)
                    if first and j == 3:
                        norm(stage)
                        act.preload_act_table_set("gelu_and_others")
                    if j == 4:
                        act.wait_ge(g_ready, n0 + 1 + i)
                        for m in range(2):
                            ins = act.activation(conv[:, m, :], g_pad[:, m, 0:SEQ], ACT.Copy,
                                                 scale=vectors[:, bass.ds(2 * i + (v_conv(layer, 0) + m), 1)])
                        ins.then_inc(tap0, 1)
                    if j == 6:
                        act.wait_ge(tap2, n0 + 1 + i)
                        for m in range(2):
                            ins = act.activation(conv[:, m, :], conv[:, m, :], ACT.Gelu,
                                                 bias=vectors[:, bass.ds(2 * i + (v_conv(layer, 3) + m), 1)])
                        ins.then_inc(gelu_done, 1)
                act.wait_ge(product, n0 + 1 + i)
                act.activation(hidden_hi[:, bass.ds(2 * i, 2), :], up[:, :, :], ACT.Copy).then_inc(hidden_hi_ready, 1)

            hidden_block(0, True)
            with act.Fori(1, FFN_BLOCKS) as i:
                hidden_block(i, False)
            act.preload_act_table_set("natural_log_exp_and_others")

            def two_blocks(i, last):
                for b in range(2):
                    for j in range(OUT_UNITS):
                        if not (last and b == 1 and j >= OUT_UNITS - RING):
                            split(U_DOWN[layer] + RING + b * OUT_UNITS + j, i, 2 * OUT_UNITS,
                                  F_SIZES[(j + RING) % OUT_UNITS])
                    if layer < DEPTH - 1:
                        residual_pair(stage + 1, 2 * i + b, V_ATTN + DC * (layer + 1))
                    else:
                        final_pair(2 * i + b)

            if layer < DEPTH - 1:
                with act.Fori(0, PAIRS // 2) as i:
                    two_blocks(i, False)
            else:
                with act.Fori(0, PAIRS // 2 - 1) as i:
                    two_blocks(i, False)
                two_blocks(PAIRS // 2 - 1, True)

        def final_pair(n):
            act.wait_ge(x_updated, PAIRS * 4 + 1 + n)
            act.wait_ge(sum_updated, (PAIRS + 1) * 4 + 1 + n)
            act.activation(squares[:, :, :], residual[:, bass.ds(2 * n, 2), :], ACT.Square).then_inc(squared, 1)
            act.wait_ge(final_copied, n + 1)
            for m in range(2):
                ins = act.activation(final_g[:, m, :], residual[:, bass.ds(2 * n + m, 1), :].rearrange("p a t -> p (a t)"),
                                     ACT.Copy, scale=vectors[:, bass.ds(2 * n + (V_FINAL + m), 1)])
            ins.then_inc(final_scaled, 1)

        feed_forward(0)

        def sub_square(p):
            act.wait_ge(sub_copied, p + 1)
            act.activation(squares[:, :, :], attended[:, :, :], ACT.Square).then_inc(sub_squared, 1)

        def sub_norm(p):
            guess_rstd(sub_norm_sems, p + 1, 1)

        def diff_head(i, first):
            for j in range(DIFF_UNITS):
                split(U_DIFF + RING + j, i, DIFF_UNITS, UK)
                if first and j == 3:
                    norm(2)
                if not first:
                    if j == 0:
                        exponents(i - 1, PAIRS)
                    if j == 5:
                        copy_probs(i - 1, PAIRS, 1)
                    if j == 8:
                        sub_square(i - 1)
                    if j == 10:
                        sub_norm(i - 1)
                    if j == 11:
                        heads_part(i - 1, PAIRS)

        diff_head(0, True)
        with act.Fori(1, PAIRS) as i:
            diff_head(i, False)

        def diff_last(j):
            if j == 0:
                exponents(PAIRS - 1, PAIRS)
            if j == 1:
                copy_probs(PAIRS - 1, PAIRS, 1)
            if j == 2:
                sub_square(PAIRS - 1)
                sub_norm(PAIRS - 1)
                heads_part(PAIRS - 1, PAIRS)

        attention_out(U_DIFF_OUT, 3, V_FFN + DC, diff_last)
        feed_forward(1)
        norm(4)
        act.wait_ge(rstd_col_ready, 3)
        act.wait_ge(final_copied, PAIRS + 1)
        act.activation(token_major[:, 0, :], token_major[:, 0, :], ACT.Copy, scale=rstd_col[:, 0:1])\
           .then_inc(final_done_act, 1)
        act.wait_ge(final_done_act, 1)
        act.dma_start(out[0, 0:P, :], token_major[:, 0, :]).then_inc(stored, 16)

    @block.vector
    def _(dve):
        dve.sem_inc(lo_ready, RING)
        dve.sem_inc(final_copied, 1)

        def split(const, i, stride, nk):
            s = const % RING
            dve.wait_ge(hi_ready, const + 1 + i * stride)
            dve.tensor_tensor(w_lo[:, s, 0:nk, :], raw[:, s, 0:nk, :], w_hi[:, s, 0:nk, :].bitcast(F32),
                              ALU.subtract).then_inc(lo_ready, 1)

        def two_wide(row):
            return row[:, None, :].to_broadcast((P, 2, SEQ))

        def residual_pair(stage, b, g_column, update):
            update(b).then_inc(x_updated, 1)
            finish_pair(stage, b, g_column)

        def finish_pair(stage, b, g_column):
            n = PAIRS * stage
            dve.wait_ge(squared, n + 1 + b)
            dve.wait_ge(sum_updated, (PAIRS + 1) * stage + 1 + b)
            dve.tensor_tensor(square_sum[:, :, :], square_sum[:, :, :], squares[:, :, :], ALU.add)\
               .then_inc(sum_updated, 1)
            if g_column is None:
                return
            dve.wait_ge(in_hi_ready, n + 1 + b)
            dve.wait_ge(x_updated, n + 1 + b)
            for m in range(2):
                chunk = bass.ds(2 * b + m, 1)
                ins = dve.scalar_tensor_tensor(in_lo[:, chunk, :], residual[:, chunk, :],
                                               vectors[:, bass.ds(2 * b + (g_column + m), 1)],
                                               in_hi[:, chunk, :].bitcast(F32), ALU.mult, ALU.subtract)
            ins.then_inc(in_ready, 1)

        def add_block(bank):
            def update(b):
                pair = residual[:, bass.ds(2 * b, 2), :]
                return dve.tensor_tensor(pair, pair, acc[bank][:, :, 0:SEQ], ALU.add)
            return update

        def take_mean(sems, wide, n, epsilon):
            sums = sum_ps[:, 0:wide * SEQ].rearrange("p (m t) -> p m t", m=wide)
            dve.tensor_scalar(mean_sq[:, 0:wide, :], sums, 1.0 / n, epsilon, ALU.mult, ALU.add)\
               .then_inc(sems["mean"], 1)

        def finish_rstd(sems, count, dst, wide, done):
            sq, mean, first = (t[:, 0:wide, :] for t in (logs, mean_sq, guess))
            dve.wait_ge(sems["guess_sq"], count)
            dve.scalar_tensor_tensor(mean, sq, -0.5, mean, ALU.mult, ALU.mult).then_inc(sems["half"], 1)
            dve.wait_ge(sems["half"], count)
            dve.scalar_tensor_tensor(dst, mean, 1.5, first, ALU.add, ALU.mult).then_inc(done, 1)
            dve.wait_ge(done, count)

        def norm(stage):
            dve.wait_ge(sums_ready, stage + 1)
            dve.memset(square_sum[:, :, :], 0.0).then_inc(sum_updated, 1)
            take_mean(token_norm, 1, D, NORM_EPS)
            finish_rstd(token_norm, stage + 1, rstd[:, None, :], 1, rstd_ready)

        def norm_column(n):
            dve.wait_ge(col_ready, n)
            dve.tensor_copy(rstd_col[:, :], out_ps[:, 0:TT]).then_inc(rstd_col_ready, 1)

        def scale_block(dst, bank):
            return dve.tensor_tensor(dst, acc[bank][:, :, 0:SEQ], two_wide(rstd), ALU.mult)

        def drain_values(bank, column_count):
            dve.wait_ge(rstd_col_ready, column_count)
            for t in range(TT):
                ins = dve.tensor_scalar(values[:, t, :], acc[bank][:, t, 0:BLOCK], rstd_col[:, t:t + 1], None, ALU.mult)
            ins.then_inc(drained, 1)

        dve.memset(square_sum[:, :, :], 0.0).then_inc(sum_updated, 1)

        def take_x(b):
            dve.wait_ge(x_t, b + 1)
            dve.tensor_copy(residual[:, 2 * b:2 * b + 2, :],
                            score_ps[:, b % 2, :].rearrange("p (m t) -> p m t", m=2)).then_inc(x_updated, 1)

        take_x(0)
        take_x(1)
        dve.wait_ge(vectors_t, 1)
        dve.tensor_copy(vectors[:, :], acc[1][:, 0, 0:VTILES * VROWS]).then_inc(vectors_ready, 1)

        dve.wait_ge(vectors_ready, 1)
        lam = vectors[:, V_LAM:V_LAM + 4].rearrange("p (a b) -> p a b", b=2)
        dve.tensor_tensor(small[:, 0:2], lam[:, :, 0], lam[:, :, 1], ALU.mult).then_inc(lam_prod, 1)
        dve.tensor_scalar(scaled[:, 0:1], vectors[:, V_QK:V_QK + 1], SCALE, None, ALU.mult).then_inc(scaled_ready, 1)
        dve.tensor_scalar(scaled[:, 1:3], vectors[:, V_SUBLN:V_SUBLN + 2], 1.0 - LAMBDA_INIT, None, ALU.mult)\
           .then_inc(scaled_ready, 1)

        for b in range(PAIRS):
            finish_pair(0, b, V_ATTN)
            if b + 2 < PAIRS:
                take_x(b + 2)
            if b in FIRST_SPLITS:
                split(FIRST_SPLITS.index(b), 0, 0, UK)
        dve.wait_ge(line_mult, 1)
        dve.tensor_copy(lines[:, :], out_ps[0:HEADS, 0:LINE]).then_inc(line_ready, 1)
        dve.wait_ge(lam_exp, 1)
        dve.tensor_tensor(small[:, 4:5], small[:, 3:4], small[:, 2:3], ALU.subtract).then_inc(lam_step, 1)
        dve.wait_ge(lam_step, 1)
        dve.tensor_scalar(small[:, 5:6], small[:, 4:5], LAMBDA_INIT, None, ALU.subtract).then_inc(lam_step, 1)
        dve.wait_ge(f_hi, 1)
        dve.tensor_tensor(heads_lo[:, :, 0:HEADS], f_raw[:, :, :], heads_hi[:, :, 0:HEADS].bitcast(F32),
                          ALU.subtract).then_inc(f_lo, 1)

        def maxima(p, n):
            dve.wait_ge(logits_done, p + 1 + n)
            dve.tensor_reduce(neg_max[:, 0:2], logits[:, :, 0:SEQ], AX.X, ALU.max, negate=True)
            dve.tensor_reduce(neg_max[:, 2:4], logits[:, :, SEQ:SCORES], AX.X, ALU.max, negate=True)\
               .then_inc(max_done, 1)

        def fox_logits(p):
            dve.wait_ge(scores_done, p + 1)
            dve.wait_ge(c_ready, 2)
            for j in range(2):
                for t, lo, hi in ((1, 0, SEQ), (0, SEQ, SCORES)):
                    c = c_col[:, t, bass.ds(2 * p + j, 1)]
                    ins = dve.scalar_tensor_tensor(logits[:, j, lo:hi], score_ps[:, j, lo:hi], c, mask[:, lo:hi],
                                                   ALU.add, ALU.add)
            ins.then_inc(logits_done, 1)
            maxima(p, 0)

        def inverse(p, n):
            dve.wait_ge(exp_done, p + 1 + n)
            dve.reciprocal(inv_sum[:, :], exp_sum[:, :]).then_inc(inv_done, 1)
            dve.wait_ge(inv_done, p + 1 + n)

        def fox_probs(p):
            inverse(p, 0)
            for j in range(2):
                for t, lo, hi in ((1, 0, SEQ), (0, SEQ, SCORES)):
                    s = j + 2 * (1 - t)
                    ins = dve.tensor_scalar(probs[:, j, lo:hi], expd[:, j, lo:hi], inv_sum[:, s:s + 1], None, ALU.mult)
            ins.then_inc(probs_done, 1)

        def fox_attended(p):
            dve.wait_ge(attended_ps, p + 1)
            dve.wait_ge(gate_ready, p + 1)
            dve.tensor_tensor(attended[:, :, :], out_ps[:, :].rearrange("p (m t) -> p m t", m=2), gate_sig[:, :, :],
                              ALU.mult).then_inc(attended_done, 1)

        def heads_part(p, n):
            dve.wait_ge(heads_hi_ready, p + 1 + n)
            dve.tensor_tensor(heads_lo[:, bass.ds(2 * p, 2), :], attended[:, :, :],
                              heads_hi[:, bass.ds(2 * p, 2), :].bitcast(F32), ALU.subtract).then_inc(heads_ready, 1)

        def fox_pair(i, first):
            if not first:
                fox_logits(i - 1)
            for j in range(FOX_UNITS):
                split(U_FOX + RING + j, i, FOX_UNITS, UK)
                if j == 2 and not first:
                    fox_probs(i - 1)
                if j == 3:
                    if first:
                        norm(0)
                    scale_block(q_raw[:, :, :], 0).then_inc(drained, 1)
                if j == 4 and first:
                    norm_column(1)
                if j == 6:
                    dve.wait_ge(q_sums, i + 1)
                    take_mean(q_norm_sems, 2, P, NORM_EPS)
                if j == 10:
                    dve.wait_ge(k_sums, i + 1)
                    take_mean(k_norm_sems, 2, P, NORM_EPS)
                if j == 7:
                    scale_block(k_raw[:, :, :], 1).then_inc(drained, 1)
                if j == 8:
                    if first:
                        dve.wait_ge(f_mult, 1)
                        dve.tensor_tensor(f_work[:, 3, :], out_ps[0:HEADS, 0:SEQ], rstd[0:HEADS, :], ALU.mult)\
                           .then_inc(f_step, 1)
                        dve.wait_ge(f_step, 1)
                        dve.tensor_scalar(f_work[:, 0, :], f_work[:, 3, :], small[0:HEADS, 8:9], None, ALU.add)\
                           .then_inc(f_abs, 1)
                    else:
                        fox_attended(i - 1)
                    finish_rstd(q_norm_sems, i + 1, head_rstd[:, :, :], 2, q_rstd)
                    dve.scalar_tensor_tensor(q_norm[:, :, :], q_raw[:, :, :], scaled[:, 0:1], head_rstd[:, :, :],
                                             ALU.mult, ALU.mult).then_inc(q_ready, 1)
                if j == 9 and not first:
                    heads_part(i - 1, 0)
                if j == 10 and first:
                    dve.wait_ge(f_act, 3)
                    dve.tensor_scalar(f_work[:, 3, :], f_work[:, 0, :], 0.0, None, ALU.min).then_inc(f_step, 1)
                    dve.wait_ge(f_step, 2)
                    dve.tensor_tensor(f_work[:, 2, :], f_work[:, 3, :], f_work[:, 1, :], ALU.subtract)\
                       .then_inc(f_step, 1)
                    dve.memset(f_work[:, 0, :], 1.0).then_inc(f_step, 1)
                    dve.wait_ge(f_step, 4)
                    dve.tensor_tensor_scan(f_work[:, 3, :], f_work[:, 0, :], f_work[:, 2, :], 0.0, ALU.mult, ALU.add)\
                       .then_inc(f_step, 1)
                if j == 11:
                    scale_block(gate[:, :, :], 0).then_inc(drained, 1)
                    finish_rstd(k_norm_sems, i + 1, head_rstd[:, :, :], 2, k_rstd)
                    dve.scalar_tensor_tensor(k_norm[:, :, :], k_raw[:, :, :], vectors[:, V_QK + 1:V_QK + 2],
                                             head_rstd[:, :, :], ALU.mult, ALU.mult).then_inc(k_ready, 1)
                if j == 12 and first:
                    dve.wait_ge(f_step, 5)
                    dve.scalar_tensor_tensor(
                        neg_c[:, :, :], f_work[:, 3, :][:, None, :].to_broadcast((HEADS, HEADS, SEQ)), -1.0,
                        identity[0:HEADS, 0:HEADS][:, :, None].to_broadcast((HEADS, HEADS, SEQ)),
                        ALU.mult, ALU.mult).then_inc(c_ready, 1)
                if j == 13:
                    if first:
                        dve.wait_ge(f_t, 1)
                        dve.tensor_copy(c_col[:, :, :], out_ps[:, 0:TT * HEADS].rearrange("p (t h) -> p t h", t=TT))\
                           .then_inc(c_ready, 1)
                    dve.wait_ge(gate_exped, i + 1)
                    dve.tensor_scalar(gate_exp[:, :, :], gate_exp[:, :, :], 1.0, None, ALU.add).then_inc(gate_step, 1)
                    dve.wait_ge(gate_step, i + 1)
                    dve.reciprocal(gate_sig[:, :, :], gate_exp[:, :, :]).then_inc(gate_ready, 1)
                if j == 15:
                    drain_values(1, 1)

        fox_pair(0, True)
        with dve.Fori(1, PAIRS) as i:
            fox_pair(i, False)

        def attention_out(u, stage, g_column, first_extra):
            def two_blocks(i, first):
                if first:
                    first_extra(None)
                for b in range(2):
                    for j in range(UD):
                        split(u + RING + b * UD + j, i, 2 * UD, UK)
                        if first and b == 0:
                            first_extra(j)
                    dve.wait_ge(multiplied, RING + u + (b + 1) * UD + i * (2 * UD))
                    residual_pair(stage, 2 * i + b, g_column, add_block(b))
            two_blocks(0, True)
            with dve.Fori(1, PAIRS // 2) as i:
                two_blocks(i, False)

        def fox_last(j):
            if j is None:
                fox_logits(PAIRS - 1)
            if j == 0:
                fox_probs(PAIRS - 1)
            if j == 2:
                fox_attended(PAIRS - 1)
                heads_part(PAIRS - 1, 0)

        attention_out(U_FOX_OUT, 1, V_FFN, fox_last)

        def feed_forward(layer):
            stage = 1 + 2 * layer
            n0 = FFN_BLOCKS * layer
            dve.wait_ge(line_stored, 16)
            dve.memset(g_pad[:, :, 0:2], 0.0).then_inc(pad_zero, 1)

            def hidden_block(i, first):
                for j in range(GU_UNITS):
                    split(U_GU[layer] + RING + j, i, GU_UNITS, UK)
                    if j == 3:
                        if first:
                            norm(stage)
                        scale_block(g_pad[:, :, 2:2 + SEQ], 0).then_inc(g_ready, 1)
                    if j == 5:
                        dve.wait_ge(tap0, n0 + 1 + i)
                        for tap, done in ((1, tap1), (2, tap2)):
                            for m in range(2):
                                ins = dve.scalar_tensor_tensor(
                                    conv[:, m, :], g_pad[:, m, tap:tap + SEQ],
                                    vectors[:, bass.ds(2 * i + (v_conv(layer, tap) + m), 1)], conv[:, m, :],
                                    ALU.mult, ALU.add)
                            ins.then_inc(done, 1)
                            if tap == 1:
                                dve.wait_ge(tap1, n0 + 1 + i)
                    if j == 7:
                        scale_block(up[:, :, :], 1).then_inc(up_ready, 1)
                        dve.wait_ge(gelu_done, n0 + 1 + i)
                        dve.wait_ge(up_ready, n0 + 1 + i)
                        dve.tensor_tensor(up[:, :, :], up[:, :, :], conv[:, :, :], ALU.mult).then_inc(product, 1)
                dve.wait_ge(hidden_hi_ready, n0 + 1 + i)
                dve.tensor_tensor(hidden_lo[:, bass.ds(2 * i, 2), :], up[:, :, :],
                                  hidden_hi[:, bass.ds(2 * i, 2), :].bitcast(F32), ALU.subtract)\
                   .then_inc(hidden_ready, 1)

            hidden_block(0, True)
            with dve.Fori(1, FFN_BLOCKS) as i:
                hidden_block(i, False)

            def two_blocks(i, last):
                for b in range(2):
                    for j in range(OUT_UNITS):
                        if not (last and b == 1 and j >= OUT_UNITS - RING):
                            split(U_DOWN[layer] + RING + b * OUT_UNITS + j, i, 2 * OUT_UNITS,
                                  F_SIZES[(j + RING) % OUT_UNITS])
                        if layer == DEPTH - 1 and j == 4:
                            if b == 1:
                                final_copy(2 * i)
                            elif not (isinstance(i, int) and i == 0):
                                final_copy(2 * i - 1)
                    dve.wait_ge(multiplied, RING + U_DOWN[layer] + (b + 1) * OUT_UNITS + i * (2 * OUT_UNITS))
                    g_column = V_ATTN + DC * (layer + 1) if layer < DEPTH - 1 else None
                    residual_pair(stage + 1, 2 * i + b, g_column, add_block(b))

            two_blocks(0, False)
            if layer < DEPTH - 1:
                with dve.Fori(1, PAIRS // 2) as i:
                    two_blocks(i, False)
            else:
                with dve.Fori(1, PAIRS // 2 - 1) as i:
                    two_blocks(i, False)
                two_blocks(PAIRS // 2 - 1, True)

        def final_copy(n):
            dve.wait_ge(final_t, n + 1)
            dve.tensor_copy(token_major[:, :, bass.ds(n * BLOCK, BLOCK)],
                            out_ps[:, :].rearrange("p (t c) -> p t c", t=TT)).then_inc(final_copied, 1)

        feed_forward(0)

        def diff_logits(p):
            dve.wait_ge(scores_done, PAIRS + 1 + p)
            dve.wait_ge(bias_landed, 16 + 16 * p)
            for j in range(2):
                for lo, hi in ((0, SEQ), (SEQ, SCORES)):
                    ins = dve.scalar_tensor_tensor(logits[:, j, lo:hi], score_ps[:, j, lo:hi], SCALE,
                                                   bias_tile[:, j, hi - lo - 1::-1], ALU.mult, ALU.add)
            ins.then_inc(logits_done, 1)
            maxima(p, PAIRS)

        def diff_probs(p):
            inverse(p, PAIRS)
            dve.tensor_scalar(inv_lam[:, :], inv_sum[:, :], small[:, 5:6], None, ALU.mult).then_inc(lam_scaled, 1)
            dve.wait_ge(lam_scaled, p + 1)
            ranges = ((0, SEQ, 0), (SEQ, SCORES, 2))
            for lo, hi, s in ranges:
                ins = dve.tensor_scalar(probs[:, 1, lo:hi], expd[:, 1, lo:hi], inv_lam[:, s + 1:s + 2], None, ALU.mult)
            ins.then_inc(probs_part, 1)
            dve.wait_ge(probs_part, p + 1)
            for lo, hi, s in ranges:
                ins = dve.scalar_tensor_tensor(probs[:, 0, lo:hi], expd[:, 0, lo:hi], inv_sum[:, s:s + 1],
                                               probs[:, 1, lo:hi], ALU.mult, ALU.add)
            ins.then_inc(probs_done, 1)

        def diff_copy(p):
            dve.wait_ge(attended_ps, PAIRS + 1 + p)
            dve.tensor_copy(attended[:, :, :], out_ps[:, :].rearrange("p (m t) -> p m t", m=2)).then_inc(sub_copied, 1)

        def diff_mean(p):
            dve.wait_ge(sub_sums, p + 1)
            take_mean(sub_norm_sems, 1, 2 * P, SUBLN_EPS)

        def diff_subln(p):
            finish_rstd(sub_norm_sems, p + 1, head_rstd[:, 0:1, :], 1, sub_rstd)
            for m in range(2):
                ins = dve.scalar_tensor_tensor(attended[:, m, :], attended[:, m, :], scaled[:, 1 + m:2 + m],
                                               head_rstd[:, 0, :], ALU.mult, ALU.mult)
            ins.then_inc(attended_done, 1)

        def diff_head(i, first):
            if not first:
                diff_logits(i - 1)
            for j in range(DIFF_UNITS):
                if j == 11:
                    dve.wait_ge(multiplied, RING + U_DIFF + DIFF_UNITS + DIFF_UNITS * i)
                    drain_values(0, 2)
                split(U_DIFF + RING + j, i, DIFF_UNITS, UK)
                if not first:
                    if j == 1:
                        diff_probs(i - 1)
                    if j == 7:
                        diff_copy(i - 1)
                    if j == 10:
                        diff_mean(i - 1)
                if j == 3:
                    if first:
                        norm(2)
                    scale_block(q_raw[:, :, :], 0).then_inc(drained, 1)
                if j == 4 and first:
                    norm_column(2)
                if j == 7:
                    scale_block(k_raw[:, :, :], 1).then_inc(drained, 1)
                if j == 11 and not first:
                    diff_subln(i - 1)
                    heads_part(i - 1, PAIRS)

        diff_head(0, True)
        with dve.Fori(1, PAIRS) as i:
            diff_head(i, False)

        def diff_last(j):
            if j is None:
                diff_logits(PAIRS - 1)
            if j == 0:
                diff_probs(PAIRS - 1)
            if j == 2:
                diff_copy(PAIRS - 1)
                diff_mean(PAIRS - 1)
                diff_subln(PAIRS - 1)
                heads_part(PAIRS - 1, PAIRS)

        attention_out(U_DIFF_OUT, 3, V_FFN + DC, diff_last)
        feed_forward(1)
        final_copy(PAIRS - 1)
        norm(4)
        norm_column(3)
        dve.wait_ge(rstd_col_ready, 3)
        dve.wait_ge(final_copied, PAIRS + 1)
        dve.tensor_scalar(token_major[:, 1, :], token_major[:, 1, :], rstd_col[:, 1:2], None, ALU.mult)\
           .then_inc(final_done, 1)

    ctx.close()


_INS = ["x", "attn_norm", "ffn_norm", "final_norm", "fox_w_in", "fox_b_f", "fox_qk_norm", "fox_w_out", "diff_w_in",
        "diff_lambda", "diff_subln", "diff_w_out", "rel_bias", "ffn_w_in", "ffn_conv_w", "ffn_conv_b", "ffn_w_out"]


def kernel(**inputs):
    import concourse.bacc as _bacc
    from concourse.bass_utils import run_bass_kernel_spmd as _run

    nc = _bacc.Bacc("TRN2", target_bir_lowering=False, num_devices=1)
    arrays, args = {}, []
    for name in _INS + ["buckets"]:
        a = bucket_table() if name == "buckets" else np.ascontiguousarray(inputs[name])
        arrays[f"in_{name}_dram"] = a
        args.append(nc.dram_tensor(f"in_{name}_dram", a.shape, mybir.dt.from_np(a.dtype), kind="ExternalInput").ap())
    args.append(nc.dram_tensor("out_0_dram", (1, SEQ, D), F32, kind="ExternalOutput").ap())
    trunk(nc, *args)
    r = _run(nc, [arrays], core_ids=[0])
    return r.results[0]["out_0_dram"]
```
